# Optimizing a Trainium2 kernel written in Bass

```python
import math
import jax, jax.numpy as jnp
from jax import lax
import numpy as np

D_MODEL = 1024
BATCH = 1
SEQ = 512
DEPTH = 1

N_BRANCH = 4
MIX_WIDTH = D_MODEL // N_BRANCH
EPS = 1e-6
Q_BLOCK = 128

A_HEAD_DIM = 64
A_HEADS = MIX_WIDTH // A_HEAD_DIM
IDX_HEADS = 8
IDX_DIM = 32
TOPK_MAX = 256

POOL_WINDOWS = (2, 4, 8, 16)
POOL_GROUPS = len(POOL_WINDOWS)
POOL_GROUP_DIM = MIX_WIDTH // POOL_GROUPS

GMLP_CHUNK = 128
GMLP_GROUPS = 4
GMLP_GROUP_DIM = MIX_WIDTH // GMLP_GROUPS

SB_HEAD_DIM = 64
SB_HEADS = MIX_WIDTH // SB_HEAD_DIM

D_FF = ((8 * D_MODEL + 3 * 256 - 1) // (3 * 256)) * 256

SPLIT_SIZES = (
    MIX_WIDTH, MIX_WIDTH, MIX_WIDTH,
    IDX_HEADS * IDX_DIM,
    IDX_DIM,
    IDX_HEADS,
    MIX_WIDTH,
    MIX_WIDTH, MIX_WIDTH,
    MIX_WIDTH, MIX_WIDTH, MIX_WIDTH,
    N_BRANCH * D_MODEL,
)
D_IN = sum(SPLIT_SIZES)

kernel_name = "hybrid_gated_dsa_pool_gmlp_stickbreak"

def _split_points():
    return [int(c) for c in np.cumsum(np.array(SPLIT_SIZES))[:-1]]

def rms_norm(x, g):
    xf = x.astype(jnp.float32)
    y = xf * lax.rsqrt(jnp.mean(xf * xf, axis=-1, keepdims=True) + EPS)
    return (y * g.astype(jnp.float32)).astype(x.dtype)

def layer_norm(x, g):
    xf = x.astype(jnp.float32)
    mu = jnp.mean(xf, axis=-1, keepdims=True)
    xc = xf - mu
    y = xc * lax.rsqrt(jnp.mean(xc * xc, axis=-1, keepdims=True) + EPS)
    return (y * g.astype(jnp.float32)).astype(x.dtype)

def sparse_indexed_attention(q, k, v, q_idx, k_idx, w_idx, q_norm, k_norm):
    B, S, H, Dh = q.shape
    topk = min(TOPK_MAX, S // 4)
    q = rms_norm(q, q_norm)
    k = rms_norm(k, k_norm)
    scale = Dh ** -0.5
    n_blocks = S // Q_BLOCK
    s_pos = jnp.arange(S)
    k_idx_f = k_idx.astype(jnp.float32)

    def block(i):
        start = i * Q_BLOCK
        qb = lax.dynamic_slice_in_dim(q, start, Q_BLOCK, axis=1)
        qib = lax.dynamic_slice_in_dim(q_idx, start, Q_BLOCK, axis=1).astype(jnp.float32)
        wb = lax.dynamic_slice_in_dim(w_idx, start, Q_BLOCK, axis=1).astype(jnp.float32)
        t_pos = start + jnp.arange(Q_BLOCK)
        head_scores = jax.nn.relu(jnp.einsum('bthd,bsd->bths', qib, k_idx_f))
        idx_score = jnp.einsum('bth,bths->bts', wb, head_scores)
        causal = s_pos[None, :] <= t_pos[:, None]
        idx_score = jnp.where(causal[None], idx_score, -jnp.inf)
        _, sel = lax.top_k(idx_score, topk)
        valid = sel <= t_pos[None, :, None]
        k_sel = jax.vmap(lambda kk, ii: kk[ii])(k, sel)
        v_sel = jax.vmap(lambda vv, ii: vv[ii])(v, sel)
        logits = jnp.einsum('bthd,btkhd->bhtk', qb, k_sel).astype(jnp.float32) * scale
        logits = jnp.where(valid[:, None], logits, -jnp.inf)
        p = jax.nn.softmax(logits, axis=-1).astype(v.dtype)
        return jnp.einsum('bhtk,btkhd->bthd', p, v_sel)

    out = lax.map(block, jnp.arange(n_blocks))
    return out.transpose(1, 0, 2, 3, 4).reshape(B, S, H * Dh)

def multiscale_pool(p, w_grp, scale):
    B, S, _ = p.shape
    pg = p.reshape(B, S, POOL_GROUPS, POOL_GROUP_DIM).astype(jnp.float32)
    csum = jnp.pad(jnp.cumsum(pg, axis=1), ((0, 0), (1, 0), (0, 0), (0, 0)))
    pos = jnp.arange(S)
    means = []
    for g, w in enumerate(POOL_WINDOWS):
        lo_idx = jnp.maximum(pos + 1 - w, 0)
        cnt = jnp.minimum(pos + 1, w).astype(jnp.float32)
        means.append((csum[:, 1:, g] - csum[:, lo_idx, g]) / cnt[None, :, None])
    pooled = jnp.stack(means, axis=2) - pg
    y = jnp.einsum('bsgc,gcd->bsgd', pooled, w_grp.astype(jnp.float32))
    return (y.reshape(B, S, MIX_WIDTH) * scale.astype(jnp.float32)).astype(p.dtype)

def chunked_spatial_gating(u, v, ln_g, w_s, b_s):
    B, S, _ = v.shape
    v = layer_norm(v, ln_g)
    vg = v.reshape(B, S // GMLP_CHUNK, GMLP_CHUNK, GMLP_GROUPS, GMLP_GROUP_DIM)
    mask = jnp.tril(jnp.ones((GMLP_CHUNK, GMLP_CHUNK), dtype=w_s.dtype))
    mixed = jnp.einsum('gts,bnsgd->bntgd', w_s * mask[None], vg)
    mixed = mixed + b_s.T[None, None, :, :, None]
    return u * mixed.reshape(B, S, MIX_WIDTH)

def stick_breaking_attention(q, k, v):
    B, S, H, Dh = q.shape
    scale = Dh ** -0.5
    n_blocks = S // Q_BLOCK
    s_pos = jnp.arange(S)

    def block(i):
        start = i * Q_BLOCK
        qb = lax.dynamic_slice_in_dim(q, start, Q_BLOCK, axis=1)
        t_pos = start + jnp.arange(Q_BLOCK)
        z = jnp.einsum('bthd,bshd->bhts', qb, k).astype(jnp.float32) * scale
        strict = (s_pos[None, :] < t_pos[:, None])[None, None]
        log_1m = jnp.where(strict, jax.nn.log_sigmoid(-z), 0.0)
        tail = lax.cumsum(log_1m, axis=3, reverse=True) - log_1m
        a = jnp.where(strict, jnp.exp(jax.nn.log_sigmoid(z) + tail), 0.0)
        return jnp.einsum('bhts,bshd->bthd', a.astype(v.dtype), v)

    out = lax.map(block, jnp.arange(n_blocks))
    return out.transpose(1, 0, 2, 3, 4).reshape(B, S, H * Dh)

def hybrid_mixer(h, w_in, q_norm, k_norm, pool_w, pool_scale,
                 gm_norm, gm_ws, gm_b, w_branch, w_out):
    B, S, _ = h.shape
    z = h @ w_in
    (aq, ak, av, iq, ik, iw, pin, gu, gv, sq, sk, sv, gl) = jnp.split(z, _split_points(), axis=-1)
    o_a = sparse_indexed_attention(
        aq.reshape(B, S, A_HEADS, A_HEAD_DIM), ak.reshape(B, S, A_HEADS, A_HEAD_DIM),
        av.reshape(B, S, A_HEADS, A_HEAD_DIM), iq.reshape(B, S, IDX_HEADS, IDX_DIM),
        ik, iw, q_norm, k_norm)
    o_b = multiscale_pool(pin, pool_w, pool_scale)
    o_c = chunked_spatial_gating(jax.nn.gelu(gu), jax.nn.gelu(gv), gm_norm, gm_ws, gm_b)
    o_d = stick_breaking_attention(
        sq.reshape(B, S, SB_HEADS, SB_HEAD_DIM), sk.reshape(B, S, SB_HEADS, SB_HEAD_DIM),
        sv.reshape(B, S, SB_HEADS, SB_HEAD_DIM))
    o = jnp.stack([o_a, o_b, o_c, o_d], axis=2)
    proj = jnp.einsum('bsnw,nwd->bsnd', o, w_branch)
    gate = jax.nn.sigmoid(gl.astype(jnp.float32)).reshape(B, S, N_BRANCH, D_MODEL)
    merged = jnp.sum(gate.astype(proj.dtype) * proj, axis=2)
    return merged @ w_out

def swiglu_ffn(h, w_gate, w_up, w_down):
    return (jax.nn.silu(h @ w_gate) * (h @ w_up)) @ w_down

def setup_inputs(seed: int = 0) -> dict:
    key = jax.random.key(seed)
    ks = jax.random.split(key, 17)
    f32 = jnp.float32

    def nrm(k, shape, s):
        return jax.random.normal(k, shape, f32) * s

    return {
        "x": nrm(ks[0], (BATCH, SEQ, D_MODEL), 1.0),
        "mix_norm": 1.0 + nrm(ks[1], (DEPTH, D_MODEL), 0.05),
        "w_in": nrm(ks[2], (DEPTH, D_MODEL, D_IN), D_MODEL ** -0.5),
        "attn_q_norm": 1.0 + nrm(ks[3], (DEPTH, A_HEAD_DIM), 0.05),
        "attn_k_norm": 1.0 + nrm(ks[4], (DEPTH, A_HEAD_DIM), 0.05),
        "pool_w": nrm(ks[5], (DEPTH, POOL_GROUPS, POOL_GROUP_DIM, POOL_GROUP_DIM), POOL_GROUP_DIM ** -0.5),
        "pool_scale": 1.0 + nrm(ks[6], (DEPTH, MIX_WIDTH), 0.05),
        "gmlp_norm": 1.0 + nrm(ks[7], (DEPTH, MIX_WIDTH), 0.05),
        "gmlp_w_s": nrm(ks[8], (DEPTH, GMLP_GROUPS, GMLP_CHUNK, GMLP_CHUNK), GMLP_CHUNK ** -0.5),
        "gmlp_b": 1.0 + nrm(ks[9], (DEPTH, GMLP_GROUPS, GMLP_CHUNK), 0.1),
        "w_branch": nrm(ks[10], (DEPTH, N_BRANCH, MIX_WIDTH, D_MODEL), MIX_WIDTH ** -0.5),
        "w_out": nrm(ks[11], (DEPTH, D_MODEL, D_MODEL), D_MODEL ** -0.5),
        "ffn_norm": 1.0 + nrm(ks[12], (DEPTH, D_MODEL), 0.05),
        "w_ffn_gate": nrm(ks[13], (DEPTH, D_MODEL, D_FF), D_MODEL ** -0.5),
        "w_ffn_up": nrm(ks[14], (DEPTH, D_MODEL, D_FF), D_MODEL ** -0.5),
        "w_ffn_down": nrm(ks[15], (DEPTH, D_FF, D_MODEL), D_FF ** -0.5),
    }

def reference(x, mix_norm, w_in, attn_q_norm, attn_k_norm, pool_w, pool_scale,
              gmlp_norm, gmlp_w_s, gmlp_b, w_branch, w_out, ffn_norm,
              w_ffn_gate, w_ffn_up, w_ffn_down):
    for l in range(DEPTH):
        h = rms_norm(x, mix_norm[l])
        x = x + hybrid_mixer(h, w_in[l], attn_q_norm[l], attn_k_norm[l], pool_w[l],
                             pool_scale[l], gmlp_norm[l], gmlp_w_s[l], gmlp_b[l],
                             w_branch[l], w_out[l])
        h = rms_norm(x, ffn_norm[l])
        x = x + swiglu_ffn(h, w_ffn_gate[l], w_ffn_up[l], w_ffn_down[l])
    return x


_drawn_inputs = setup_inputs


def setup_inputs(seed=0):
    import zlib

    import numpy as np

    out = dict(_drawn_inputs(seed))
    spreads = {}
    factors = {'attn_q_norm': 8.0,
     'attn_k_norm': 8.0,
     'gmlp_norm': 5.109,
     'pool_scale': 3.996,
     'gmlp_b': 2.821,
     'ffn_norm': 3.755}
    for name, (base, spread) in spreads.items():
        noise = np.random.default_rng([zlib.crc32(name.encode()), seed]).standard_normal(out[name].shape)
        drawn = base * np.exp(spread * noise) if base else spread * noise
        out[name] = __import__('jax').numpy.asarray(drawn.astype(out[name].dtype))
    for name, factor in factors.items():
        out[name] = (out[name] * factor).astype(out[name].dtype)
    return out
```

```python
from contextlib import ExitStack

import concourse.bass as bass
from concourse import mybir

ALU = mybir.AluOpType
ACT = mybir.ActivationFunctionType
AX = mybir.AxisListType
F32 = mybir.dt.float32
F32R = mybir.dt.float32r
BF16 = mybir.dt.bfloat16

P = 128
EPS = 1e-6
TOPK = 128
POOL_WINDOWS = (2, 4, 8, 16)
PAD = POOL_WINDOWS[-1]
HEADS = 4
HEAD_DIM = 64
IDX_HEADS = 8
IDX_DIM = 32
OUTSIDE = -3.0e38
TAKEN = -3.4e38
BETWEEN = -3.2e38
MASKED = -1.0e30


def hybrid_layer(nc, x, mix_norm, w_in, attn_q_norm, attn_k_norm, pool_w, pool_scale, gmlp_norm,
                 gmlp_w_s, gmlp_b, w_branch, w_out, ffn_norm, w_ffn_gate, w_ffn_up, w_ffn_down, out):
    _, SEQ, D = x.shape
    N_BRANCH, MIX = w_branch.shape[1:3]
    D_FF = w_ffn_gate.shape[2]
    TT = SEQ // P
    KT = D // P
    FT = D_FF // P
    MT = MIX // P
    CW = 256
    CT = CW // P
    CHUNK = KT * CW
    HALF = D // 2
    KC = CHUNK // HALF
    SCALE = float(HEAD_DIM) ** -0.5
    assert SEQ == 512 and D == 1024 and MIX == 256 and TT * P == SEQ

    widths = [MIX, MIX, MIX, IDX_HEADS * IDX_DIM, IDX_DIM, IDX_HEADS, MIX, MIX, MIX, MIX, MIX, MIX]
    names = ["aq", "ak", "av", "iq", "ik", "iw", "pin", "gu", "gv", "sq", "sk", "sv"]
    col = {n: sum(widths[:i]) for i, n in enumerate(names)}
    col["gl"] = sum(widths)

    def in_cols(w, c0, n=CW):
        return w[0, :, c0:c0 + n].rearrange("(k p) c -> p k c", p=P)

    chunks = []
    chunks.append(("rows", in_cols(w_in, col["ik"], P), KT, P, "ik"))
    chunks.append(("rows", in_cols(w_in, col["iq"]), KT, CW, "iq"))
    for n in ("aq", "ak", "av", "gv"):
        chunks.append(("toks", in_cols(w_in, col[n]), KT, CW, n))
    for n in ("gu", "pin", "sq", "sk"):
        chunks.append(("rows", in_cols(w_in, col[n]), KT, CW, n))
    chunks.append(("toks", in_cols(w_in, col["sv"]), KT, CW, "sv"))
    BRANCHES = (2, 1, 3, 0)
    O_SET = (0, 1, 2, 0)
    for m, n in enumerate(BRANCHES):
        for q in range(D // CW):
            chunks.append(("rows", in_cols(w_in, col["gl"] + n * D + q * CW), KT, CW, ("gate", m, q)))
        chunks.append(("proj", w_branch[0, n].rearrange("(k p) d -> p k d", p=P), MT, D, m))

    def acc_chunks(w, k0, nk, group):
        for half in range(2):
            for k in range(0, nk, KC):
                kn = min(KC, nk - k)
                src = w[0, (k0 + k) * P:(k0 + k + kn) * P, half * HALF:(half + 1) * HALF]
                chunks.append(("acc", src.rearrange("(k p) d -> p k d", p=P), kn, HALF,
                               (group + half, k, k == 0, k + kn == nk)))

    acc_chunks(w_out, 0, KT, 0)
    MIXER_CHUNKS = len(chunks)
    PROJ_AT = [c for c in range(MIXER_CHUNKS) if chunks[c][0] == "proj"]
    PAIRS = [(D_FF // CW + 1) // 2, D_FF // CW // 2]
    FF_PART = CT * PAIRS[0]
    part_at, down_at = [], []
    for part, pairs in enumerate(PAIRS):
        part_at.append(len(chunks))
        for i in range(pairs):
            for w in (w_ffn_gate, w_ffn_up):
                chunks.append(("ffn", in_cols(w, (part * PAIRS[0] + i) * CW), KT, CW, None))
        down_at.append(len(chunks))
        acc_chunks(w_ffn_down, part * FF_PART, CT * pairs, 2 + 2 * part)
    NC = len(chunks)

    fill_at, f = [], 0
    for kind, _, _, cols, _ in chunks:
        fill_at.append(f)
        f += {"rows": cols // P, "toks": 2, "proj": KT, "acc": 0, "ffn": CT}[kind]
    fill_at.append(f)

    with ExitStack() as ctx:
        top = [(nc.sbuf_base + 63) // 64 * 64]

        def place(name, shape, dt=F32, at=None):
            size = 4
            for n in shape[1:]:
                size *= n
            if at is None:
                at = top[0]
                top[0] += (size + 63) // 64 * 64
            return nc.alloc_sbuf_tensor_at(name, shape, dt, offset=at)

        def sem(name):
            return ctx.enter_context(nc.semaphore(name))

        KB = 1024
        X0 = top[0]
        x_sb = place("x_sb", [P, TT, D])
        gv = place("gv", [P, TT, MIX], at=X0)
        gu = place("gu", [P, MT, SEQ], at=X0 + 4 * KB)
        mixed = place("mixed", [P, MT, SEQ], at=X0 + 8 * KB)
        sv = place("sv", [P, TT, MIX], at=X0 + 12 * KB)
        h_hi = place("h_hi", [P, KT, SEQ], F32R)
        h_lo = place("h_lo", [P, KT, SEQ], F32R)
        raw = place("raw", [P, 2, CHUNK])
        w_hi = place("w_hi", [P, 2, CHUNK], F32R)
        w_lo = place("w_lo", [P, 2, CHUNK], F32R)
        L0 = top[0]
        gates = place("gates", [P, KT, SEQ])
        merged = place("merged", [P, KT, SEQ])
        o_hi = place("o_hi", [P, 3, MT, SEQ], F32R)
        o_lo = place("o_lo", [P, 3, MT, SEQ], F32R)
        act_junk = place("act_junk", [P, 2, D], at=L0)
        dve_junk = place("dve_junk", [P, 2, D], at=L0 + 20 * KB)
        qk = place("qk", [P, 2, TT, MIX], at=L0)
        iq_hi = place("iq_hi", [P, 2, SEQ], F32R, at=L0 + 32 * KB)
        iq_lo = place("iq_lo", [P, 2, SEQ], F32R, at=L0 + 36 * KB)
        sq_tmp = place("sq_tmp", [P, TT, MIX], at=L0 + 8 * KB)
        PW = PAD + SEQ
        pin = place("pin", [P, MT, PW], at=L0 + 12 * KB)
        s2 = place("s2", [P, MT, PW], at=L0 + 12 * KB + 8 * PW)
        s4 = place("s4", [P, MT, PW], at=L0 + 12 * KB + 16 * PW)
        s8 = place("s8", [P, 1, PW], at=L0 + 12 * KB + 24 * PW)
        s16 = place("s16", [P, 1, PW], at=L0 + 12 * KB + 28 * PW)
        h2 = place("h2", [P, TT, D], at=L0)
        ffn_gain = place("ffn_gain", [P, D], at=L0 + 16 * KB)
        a_hi = place("a_hi", [P, FF_PART, SEQ], F32R, at=L0)
        a_lo = place("a_lo", [P, FF_PART, SEQ], F32R, at=L0 + FF_PART * SEQ * 4)
        two = place("two", [P, 2, SEQ])
        qT = place("qT", [P, MT, SEQ])
        kT = place("kT", [P, MT, SEQ])
        av = place("av", [P, TT, MIX])
        q_stack = place("q_stack", [P, HEADS, SEQ], F32R, at=X0)
        q_lo = place("q_lo", [P, MT, SEQ], F32R, at=X0 + 8 * KB)
        k_stack = place("k_stack", [P, HEADS, SEQ], F32R)
        a32 = place("a32", [P, CT, SEQ], at=top[0] - 8 * KB)
        score_at = [0, 0, 2 * P, 5 * P]
        score = place("score", [P, 9 * P])
        S0 = top[0]
        iq_stack = place("iq_stack", [P, IDX_HEADS, SEQ], F32R, at=X0)
        ik_stack = place("ik_stack", [P, SEQ], F32R)
        ikw = place("ikw", [P, SEQ])
        top[0] += 4 * KB
        relu = place("relu", [P, 4, SEQ])
        stick_buf = place("stick", [P, 1280], at=S0)
        stick_lo = place("stick_lo", [P, 1280], F32R, at=S0)
        beta = place("beta", [P, 1280], at=S0 + 5 * KB)
        stick_hi = place("stick_hi", [P, 1280], F32R, at=S0 + 10 * KB)
        prob = place("prob", [P, HEADS, SEQ], at=S0)
        probT = place("probT", [P, HEADS, SEQ], at=S0 + 8 * KB)
        ident = place("ident", [P, P])
        identb = place("identb", [P, P], BF16)
        later = place("later", [P, P], BF16)
        neg_tri = place("neg_tri", [P, P])
        neg_one = place("neg_one", [P, P])
        tri_r = place("tri_r", [P, P], F32R)
        one_r = place("one_r", [P, P], F32R)
        causal = place("causal", [P, SEQ])
        vrow = place("vrow", [2 * KT + 6, P])
        vcol = place("vcol", [P, 2 * KT + 6])
        ws = place("ws", [P, 4, P], at=S0 + 12 * KB)
        wsT = place("wsT", [P, 4, P])
        gb = place("gb", [P, MT, P])
        pw = place("pw", [P, MT, HEAD_DIM])
        iw = place("iw", [P, TT, IDX_HEADS])
        ramp = place("ramp", [P, MT, PAD])
        window = place("window", [P, MT])
        inv_window = place("inv_window", [P, MT])
        stat = place("stat", [P, 32])
        root = place("root", [P, 32])
        rstd = place("rstd", [P, 32])
        newton = place("newton", [P, 32])
        sums = place("sums", [P, 2 * TT])
        bn = place("bn", [P, TT, 6])
        mv = place("mv", [P, TT, 2])
        best = place("best", [P, 8])
        top_logit = place("top_logit", [P, HEADS])
        neg_top = place("neg_top", [P, HEADS])
        total = place("total", [P, HEADS])
        inv_total = place("inv_total", [P, HEADS])
        assert top[0] <= nc.sbuf_usable_end, (top[0], nc.sbuf_usable_end)
        MIXN, FFNN, PSC, GMN, QN, KN = 0, KT, 2 * KT, 2 * KT + 2, 2 * KT + 4, 2 * KT + 5

        bank = [ctx.enter_context(nc.psum_tensor(f"bank{i}", [P, 512], F32)) for i in range(8)]

        def acc_bank(a):
            return bank[2 + a % 6]

        names = """raw0 raw1 hi_ready lo_ready acc_chunks filled taken0 taken1
            x0 x1s x2 x3 vec_in ws_in gb_in pw_in gain_in x_back const_made corr_made tril_made
            squares_summed var_ready root_ready dve_step pool_step act_step
            rstd_ready h_scaled h_last_scaled h_turned h_hi_ready h_lo_ready vec_turned ws_ready ws_turned
            iw_turned iw_ready ik_hi_ready iq_hi_ready iq_stacked idx_filled relu_ready signs_ready q_hi_ready k_hi_ready stacks_ready relu_used
            qk_scaled qk_turned qk_evac
            v_normed mix_filled mixed_ready windows_summed pooled_ready pool_filled
            o_hi_ready o_lo_ready sb_filled softplus_ready stick_ready stick_hi_ready stick_lo_ready tail_filled beta_ready sb_out
            bias_ready logits_filled biased_ready neg_top_ready prob_summed prob_ready prob_turned
            probT_ready attn_out proj_added mg_hi_ready mg_lo_ready
            acc_filled x1_taken h2_scaled h2_turned h2_hi_ready h2_lo_ready
            a_hi_ready a_lo_ready stored""".split()
        S = {n: sem(n) for n in names}
        taken = [S["taken0"], S["taken1"]]
        raw_ready = [S["raw0"], S["raw1"]]
        x_ready = [S["x0"], S["x1s"], S["x2"], S["x3"]]
        hi_ready, lo_ready, filled = S["hi_ready"], S["lo_ready"], S["filled"]

        block = ctx.enter_context(nc.Block())

        O_DONE = (2, 4, 8, 10)
        D_SLOT, A_SLOT = 10, 16
        IDX_SLOT = 2

        def split_early(c):
            return IDX_SLOT <= c - 2 < IDX_SLOT + 3

        def wait_taken(eng, f):
            eng.wait_ge(taken[f % 2], f // 2 + 1)

        def wait_chunk_taken(eng, c):
            for f in range(max(fill_at[c + 1] - 2, fill_at[c]), fill_at[c + 1]):
                wait_taken(eng, f)

        def wait_used(eng, c):
            kind, _, _, _, what = chunks[c]
            if kind != "acc":
                eng.wait_ge(filled, fill_at[c + 1])
            elif what[3]:
                eng.wait_ge(S["acc_filled"], TT * (what[0] + 1))
            else:
                eng.wait_ge(S["acc_chunks"], sum(k[0] == "acc" and not k[4][3] for k in chunks[:c + 1]))

        @block.sync
        def _(sp):
            for t in range(TT):
                sp.dma_start(x_sb[:, t, :], x[0, t * P:(t + 1) * P, :]).then_inc(x_ready[t], 16)

            def load(c):
                _, src, nk, cols, _ = chunks[c]
                if c >= 2:
                    sp.wait_ge(lo_ready, c - 1)
                dst = raw[:, c % 2, 0:nk * cols].rearrange("p (k c) -> p k c", c=cols)
                sp.dma_start(dst, src).then_inc(raw_ready[c % 2], 16)

            load(0)
            sp.dma_start(vrow[0:KT, :], mix_norm[0].rearrange("(k p) -> k p", p=P)).then_inc(S["vec_in"], 16)
            sp.dma_start(vrow[KT:2 * KT, :], ffn_norm[0].rearrange("(k p) -> k p", p=P)).then_inc(S["vec_in"], 16)
            sp.dma_start(vrow[PSC:PSC + 2, :], pool_scale[0].rearrange("(k p) -> k p", p=P)).then_inc(S["vec_in"], 16)
            sp.dma_start(vrow[GMN:GMN + 2, :], gmlp_norm[0].rearrange("(k p) -> k p", p=P)).then_inc(S["vec_in"], 16)
            for r, g in ((QN, attn_q_norm), (KN, attn_k_norm)):
                for j in range(2):
                    sp.dma_start(vrow[r:r + 1, j * HEAD_DIM:(j + 1) * HEAD_DIM], g).then_inc(S["vec_in"], 16)
            for c in range(1, MIXER_CHUNKS):
                load(c)
                if c == 4:
                    wait_chunk_taken(sp, 1)
                    for block_, part in enumerate((iq_hi, iq_lo, iq_hi)):
                        for q in range(4):
                            sp.dma_start(iq_stack[32 * block_:32 * block_ + 32, q::4, :].bitcast(F32),
                                         part[32 * q:32 * q + 32, :, :].bitcast(F32))\
                                .then_inc(S["iq_stacked"], 16)
                if c == 26:
                    sp.wait_ge(S["o_lo_ready"], O_DONE[2])
                    sp.wait_ge(S["logits_filled"], HEADS * TT)
                    sp.dma_start(x_sb[:, :, :], x[0].rearrange("(t p) d -> p t d", p=P)).then_inc(S["x_back"], 16)
            sp.wait_ge(S["mg_lo_ready"], KT)
            sp.dma_start(ffn_gain[:, :], ffn_norm[0:1, :].broadcast_to([P, D])).then_inc(S["gain_in"], 16)
            for part, pairs in enumerate(PAIRS):
                at = part_at[part]
                with sp.Fori(0, pairs) as i:
                    for s, w in enumerate((w_ffn_gate, w_ffn_up)):
                        sp.wait_ge(lo_ready, 2 * i + (at + s - 1))
                        src = w[0][:, bass.ds((i + part * PAIRS[0]) * CW, CW)].rearrange("(k p) c -> p k c", p=P)
                        dst = raw[:, (at + s) % 2, :].rearrange("p (k c) -> p k c", c=CW)
                        sp.dma_start(dst, src).then_inc(raw_ready[(at + s) % 2], 16)
                for c in range(down_at[part], part_at[1] if part == 0 else NC):
                    load(c)
            for tile in range(2 * TT):
                half, t = tile // TT, tile % TT
                sp.wait_ge(S["x1_taken"], 4 * TT + tile + 1)
                sp.dma_start(out[0, t * P:(t + 1) * P, half * HALF:(half + 1) * HALF],
                             x_sb[:, t, half * HALF:(half + 1) * HALF]).then_inc(S["stored"], 16)
            sp.wait_ge(S["stored"], 16 * 2 * TT)

        @block.gpsimd
        def _(pool):
            steps = [0]

            def link(ins):
                steps[0] += 1
                ins.then_inc(S["pool_step"], 1)
                pool.wait_ge(S["pool_step"], steps[0])

            link(pool.memset(ident[:, :], 0.0))
            pool.affine_select(out=ident[:, :], in_=ident[:, :], compare_op=ALU.not_equal, fill=1.0, base=0,
                               pattern=[[-1, P]], channel_multiplier=1).then_inc(S["const_made"], 1)
            link(pool.memset(identb[:, :], 0.0))
            pool.affine_select(out=identb[:, :], in_=identb[:, :], compare_op=ALU.not_equal, fill=1.0, base=0,
                               pattern=[[-1, P]], channel_multiplier=1).then_inc(S["const_made"], 1)
            link(pool.memset(later[:, :], 0.0))
            pool.affine_select(out=later[:, :], in_=later[:, :], compare_op=ALU.is_gt, fill=MASKED, base=0,
                               pattern=[[1, P]], channel_multiplier=-1).then_inc(S["const_made"], 1)
            pool.memset(neg_one[:, :], -1.0).then_inc(S["const_made"], 1)
            link(pool.memset(neg_tri[:, :], -1.0))
            pool.affine_select(out=neg_tri[:, :], in_=neg_tri[:, :], compare_op=ALU.is_ge, fill=0.0, base=0,
                               pattern=[[-1, P]], channel_multiplier=1).then_inc(S["const_made"], 1)
            link(pool.memset(causal[:, :], 0.0))
            diag = causal[:, SEQ - P:SEQ]
            pool.affine_select(out=diag, in_=diag, compare_op=ALU.is_ge, fill=OUTSIDE, base=0,
                               pattern=[[-1, P]], channel_multiplier=1).then_inc(S["const_made"], 1)
            pool.dma_start(ws[:, :, :], gmlp_w_s[0].rearrange("g t s -> t g s")).then_inc(S["ws_in"], 16)
            for g in range(4):
                pool.dma_start(gb[(g % 2) * 64:(g % 2) * 64 + 64, g // 2, :],
                               gmlp_b[0, g:g + 1, :].broadcast_to([64, P])).then_inc(S["gb_in"], 16)
                pool.dma_start(pw[(g % 2) * 64:(g % 2) * 64 + 64, g // 2, :], pool_w[0, g]).then_inc(S["pw_in"], 16)
            pool.wait_ge(S["ws_in"], 16)
            pool.affine_select(out=ws[:, :, :], in_=ws[:, :, :], compare_op=ALU.is_ge, fill=0.0, base=0,
                               pattern=[[0, 4], [-1, P]], channel_multiplier=1).then_inc(S["tril_made"], 1)
            link(pool.iota(ramp[:, :, :], pattern=[[0, MT], [1, PAD]], base=1, channel_multiplier=0,
                      allow_small_or_imprecise_dtypes=True))
            for g, w in enumerate(POOL_WINDOWS):
                rows = slice((g % 2) * 64, (g % 2) * 64 + 64)
                link(pool.memset(window[rows, g // 2:g // 2 + 1], float(w)))
                link(pool.memset(inv_window[rows, g // 2:g // 2 + 1], 1.0 / w))
            for i in range(MT):
                last = pool.tensor_scalar(ramp[:, i, :], ramp[:, i, :], window[:, i:i + 1], None, ALU.min)
            last.then_inc(S["corr_made"], 1)

            link(pool.memset(pin[:, :, 0:PAD], 0.0))
            wait_chunk_taken(pool, 7)
            link(pool.tensor_tensor(s2[:, :, 1:PW], pin[:, :, 1:PW], pin[:, :, 0:PW - 1], ALU.add))
            link(pool.tensor_tensor(s4[:, :, 3:PW], s2[:, :, 3:PW], s2[:, :, 1:PW - 2], ALU.add))
            link(pool.tensor_tensor(s8[:, 0, 7:PW], s4[:, 1, 7:PW], s4[:, 1, 3:PW - 4], ALU.add))
            pool.tensor_tensor(s16[:, 0, 15:PW], s8[:, 0, 15:PW], s8[:, 0, 7:PW - 8], ALU.add)\
                .then_inc(S["windows_summed"], 1)

            for m in range(1, N_BRANCH):
                for d in range(KT):
                    y = (m - 1) * KT + d
                    wait_taken(pool, fill_at[PROJ_AT[m]] + d)
                    if m > 1:
                        pool.wait_ge(S["proj_added"], y + 1 - KT)
                    pool.tensor_tensor(merged[:, d, :], merged[:, d, :], two[:, y % 2, :], ALU.add)\
                        .then_inc(S["proj_added"], 1)

        @block.scalar
        def _(act):
            nact = nc.scalar
            steps = [0]

            def link(ins):
                steps[0] += 1
                ins.then_inc(S["act_step"], 1)
                act.wait_ge(S["act_step"], steps[0])

            def split(c):
                n = chunks[c][2] * chunks[c][3]
                act.wait_ge(raw_ready[c % 2], 16 * (c // 2 + 1))
                if c >= 2:
                    wait_used(act, c - 2)
                nact.activation(w_hi[:, c % 2, 0:n], raw[:, c % 2, 0:n], ACT.Copy).then_inc(hi_ready, 1)

            roots = [0]

            def take_root(at):
                roots[0] += 1
                act.wait_ge(S["var_ready"], roots[0])
                nact.activation(root[:, at], stat[:, at], ACT.Sqrt).then_inc(S["root_ready"], 1)

            for t in (0, 2):
                act.wait_ge(x_ready[t], 16)
                nact.activation(act_junk[:, t // 2, :], x_sb[:, t, :], ACT.Square, accum_out=stat[:, t:t + 1])\
                    .then_inc(S["squares_summed"], 1)
            take_root(slice(0, TT))
            split(0)
            act.wait_ge(S["rstd_ready"], 1)
            nact.activation(x_sb[:, TT - 1, :], x_sb[:, TT - 1, :], ACT.Copy, scale=rstd[:, TT - 1:TT])\
                .then_inc(S["h_last_scaled"], 1)
            act.wait_ge(S["vec_turned"], 1)
            link(nact.activation(vcol[:, :], bank[1][:, 0:2 * KT + 6], ACT.Copy))
            for k in range(KT):
                act.wait_ge(S["h_turned"], k + 1)
                nact.activation(h_hi[:, k, :], bank[2 + k % 6][:, :], ACT.Copy, scale=vcol[:, MIXN + k:MIXN + k + 1])\
                    .then_inc(S["h_hi_ready"], 1)

            def stack_high(queries, src, heads, scale):
                for x in range(2):
                    own = slice(64 * x, 64 * x + 64)
                    for rows in (slice(0, 64), slice(64, 128)) if queries else (own,):
                        ins = nact.activation((q_stack if queries else k_stack)[rows, heads(x), :], src[own], ACT.Copy,
                                              scale=scale)
                ins.then_inc(S["q_hi_ready" if queries else "k_hi_ready"], 1)

            def evac(c):
                kind, _, _, _, what = chunks[c]
                for f in range(fill_at[c], fill_at[c + 1]):
                    j = f - fill_at[c]
                    b = bank[f % 2]
                    act.wait_ge(filled, f + 1)
                    if what == "ik":
                        for q in range(2):
                            nact.activation(ik_stack[32 * q:32 * q + 32, :], b[0:32, :], ACT.Copy)
                        nact.activation(ikw[32:64, :], b[32:64, :], ACT.Copy).then_inc(S["ik_hi_ready"], 1)
                        continue
                    wide = b[:, :]
                    toks = b[:, :].rearrange("p (t c) -> p t c", t=2)
                    if what == "iq":
                        nact.activation(iq_hi[:, j, :], wide, ACT.Copy).then_inc(S["iq_hi_ready"], 1)
                        continue
                    if what in ("aq", "ak"):
                        ins = nact.activation(qk[:, int(what == "ak"), 2 * j:2 * j + 2, :], toks, ACT.Copy)
                    elif what == "av":
                        ins = nact.activation(av[:, 2 * j:2 * j + 2, :], toks, ACT.Copy)
                    elif what == "gv":
                        ins = nact.activation(gv[:, 2 * j:2 * j + 2, :], toks, ACT.Gelu_apprx_tanh)
                    elif what == "gu":
                        ins = nact.activation(gu[:, j, :], wide, ACT.Gelu_apprx_tanh)
                    elif what == "pin":
                        ins = nact.activation(pin[:, j, PAD:PW], wide, ACT.Copy)
                    elif what in ("sq", "sk"):
                        stack_high(what == "sq", b, lambda x: 2 * j + x, SCALE if what == "sq" else 1.0)
                        continue
                    elif what == "sv":
                        ins = nact.activation(sv[:, 2 * j:2 * j + 2, :], toks, ACT.Copy)
                    else:
                        _, m, q = what
                        if m == 0 and q == 0 and j == 0:
                            act.wait_ge(S["pool_filled"], 1)
                        elif m > 0 and q == 0 and j == 0:
                            wait_chunk_taken(act, c - 1)
                        ins = nact.activation(gates[:, CT * q + j, :], wide, ACT.Sigmoid)
                    ins.then_inc(taken[f % 2], 1)

            def indexer(b):
                for h in range(IDX_HEADS):
                    n = IDX_HEADS * (b - 1) + h
                    act.wait_ge(S["idx_filled"], n + 1)
                    if n >= 4:
                        act.wait_ge(S["relu_used"], n - 3)
                    w = P * (b + 1)
                    nact.activation(relu[:, n % 4, 0:w], bank[2 + n % 4][:, 0:w], ACT.Relu).then_inc(S["relu_ready"], 1)

            def turned_qk():
                for i in range(4):
                    which, pair = i // 2, i % 2
                    act.wait_ge(S["qk_turned"], i + 1)
                    v = (QN, KN)[which]
                    nact.activation((qT, kT)[which][:, pair, :], bank[6 + pair][:, :], ACT.Copy,
                                    scale=vcol[:, v:v + 1]).then_inc(S["qk_evac"], 1)

            def softplus(h):
                if h == 0:
                    act.wait_ge(S["relu_used"], 3 * IDX_HEADS)
                act.wait_ge(S["sb_filled"], h + 1)
                if h >= 1:
                    act.wait_ge(S["tail_filled"], h)
                for i, (a, z) in enumerate(((0, 512), (512, 1024), (1024, 1280))):
                    last = nact.activation(stick_buf[:, a:z], bank[2 + 3 * (h % 2) + i][:, 0:z - a], ACT.Abs)
                link(last)
                link(nact.activation(stick_buf[:, :], stick_buf[:, :], ACT.Exp, scale=-1.0))
                nact.activation(stick_buf[:, :], stick_buf[:, :], ACT.Ln, bias=1.0).then_inc(S["softplus_ready"], 1)

            def stick_high(h):
                for i, (a, z) in enumerate(((0, 512), (512, 1024), (1024, 1280))):
                    act.wait_ge(S["stick_ready"], 3 * h + i + 1)
                    nact.activation(stick_hi[:, a:z], stick_buf[:, a:z], ACT.Copy).then_inc(S["stick_hi_ready"], 1)

            def breaking(h):
                act.wait_ge(S["tail_filled"], h + 1)
                if h >= 1:
                    act.wait_ge(S["sb_out"], h)
                for i, (a, z) in enumerate(((0, 512), (512, 1024), (1024, 1280))):
                    nact.activation(beta[:, a:z], bank[2 + 3 * (h % 2) + i][:, 0:z - a], ACT.Exp)\
                        .then_inc(S["beta_ready"], 1)

            def stick_out(h):
                act.wait_ge(S["sb_out"], h + 1)
                r = slice(64 * (h % 2), 64 * (h % 2) + 64)
                nact.activation(o_hi[r, O_SET[2], h // 2, :], bank[2 + 3 * (h % 2)][r, :], ACT.Copy)\
                    .then_inc(S["o_hi_ready"], 1)

            def soft_max(b):
                w = P * (b + 1)
                act.wait_ge(S["biased_ready"], HEADS * (b + 1))
                link(nact.mul(neg_top[:, :], top_logit[:, :], -1.0))
                for h in range(HEADS):
                    nact.activation(prob[:, h, 0:w], prob[:, h, 0:w], ACT.Exp, bias=neg_top[:, h:h + 1],
                                    accum_out=total[:, h:h + 1]).then_inc(S["prob_summed"], 1)

            def turned_prob(b):
                w = P * (b + 1)
                for h in range(HEADS):
                    act.wait_ge(S["prob_turned"], HEADS * b + h + 1)
                    if h == 0 and b >= 1:
                        act.wait_ge(S["attn_out"], b)
                    nact.activation(probT[:, h, 0:w], bank[2 + h][:, 0:w], ACT.Copy).then_inc(S["probT_ready"], 1)

            def out_parts(filled_sem, count, branch, b0, scale):
                for i in range(MT):
                    act.wait_ge(filled_sem, count)
                    s = {} if scale is None else {"scale": vcol[:, scale + i:scale + i + 1]}
                    nact.activation(o_hi[:, O_SET[branch], i, :], bank[b0 + i][:, :], ACT.Copy, **s)\
                        .then_inc(S["o_hi_ready"], 1)

            def slot(c):
                if IDX_SLOT <= c < IDX_SLOT + 3:
                    if c == 4:
                        take_root(slice(0, 32))
                    indexer(c - IDX_SLOT + 1)
                if c == 1:
                    act.wait_ge(S["ws_turned"], 1)
                    nact.activation(wsT[:, :, :], bank[7][:, :].rearrange("p (g t) -> p g t", g=4), ACT.Copy)\
                        .then_inc(S["ws_ready"], 1)
                    act.wait_ge(S["iw_turned"], 1)
                    nact.activation(iw[:, :, :], bank[6][:, 0:TT * IDX_HEADS].rearrange("p (t h) -> p t h", t=TT),
                                    ACT.Copy).then_inc(S["iw_ready"], 1)
                if c == 5:
                    turned_qk()
                    take_root(slice(0, TT))
                if c == 7:
                    act.wait_ge(S["mixed_ready"], 1)
                    for i in range(MT):
                        nact.activation(o_hi[:, O_SET[0], i, :], mixed[:, i, :], ACT.Copy).then_inc(S["o_hi_ready"], 1)
                if c == 9:
                    out_parts(S["pool_filled"], 1, 1, 6, PSC)
                if D_SLOT <= c < D_SLOT + HEADS + 2:
                    k = c - D_SLOT
                    if k == 0:
                        nact.preload_act_table_set("natural_log_exp_and_others")
                    if k >= 2:
                        stick_out(k - 2)
                    if 1 <= k <= HEADS:
                        breaking(k - 1)
                    if k < HEADS:
                        softplus(k)
                        stick_high(k)
                if A_SLOT <= c <= A_SLOT + 2 * TT:
                    b, odd = (c - A_SLOT) // 2, (c - A_SLOT) % 2
                    if odd:
                        turned_prob(b)
                    elif b < TT:
                        soft_max(b)
                    else:
                        wait_used(act, PROJ_AT[0])
                        out_parts(S["attn_out"], TT, 3, 6, None)

            for c in range(MIXER_CHUNKS):
                if c + 1 < MIXER_CHUNKS and not split_early(c + 1):
                    split(c + 1)
                if chunks[c][0] in ("rows", "toks"):
                    evac(c)
                if split_early(c + 2):
                    split(c + 2)
                if c == D_SLOT + HEADS + 1:
                    act.wait_ge(S["sb_filled"], HEADS)
                    for queries, src in ((True, qT), (False, kT)):
                        stack_high(queries, src, lambda x: slice(x, HEADS, 2), 1.0)
                if chunks[c][0] == "proj" and chunks[c][4] == N_BRANCH - 1:
                    for d in range(KT):
                        act.wait_ge(S["proj_added"], (N_BRANCH - 2) * KT + d + 1)
                        nact.activation(h_hi[:, d, :], merged[:, d, :], ACT.Copy).then_inc(S["mg_hi_ready"], 1)
                slot(c)

            def h2_high(t):
                for half in range(2):
                    act.wait_ge(S["h2_turned"], 2 * t + half + 1)
                    ks = slice(half * KT // 2, (half + 1) * KT // 2)
                    nact.activation(h_hi[:, ks, t * P:(t + 1) * P],
                                    bank[4 + half][:, :].rearrange("p (k t) -> p k t", t=P), ACT.Copy)\
                        .then_inc(S["h2_hi_ready"], 1)

            def square(a):
                t, half = a % TT, a // TT
                act.wait_ge(S["x1_taken"], a + 1)
                if a >= 2:
                    act.wait_ge(S["squares_summed"], a + 1)
                nact.activation(two[:, a % 2, :], x_sb[:, t, half * HALF:(half + 1) * HALF], ACT.Square,
                                accum_out=sums[:, a:a + 1]).then_inc(S["squares_summed"], 1)

            act.wait_ge(S["proj_added"], (N_BRANCH - 1) * KT)
            for a in range(TT):
                square(a)
            for t in range(TT):
                if t == 2:
                    split(MIXER_CHUNKS)
                square(TT + t)
                take_root(slice(t, t + 1))
                if t > 0:
                    h2_high(t - 1)
            h2_high(TT - 1)

            for part, pairs in enumerate(PAIRS):
                at, f0 = part_at[part], fill_at[part_at[part]]
                wait_used(act, at - 1)
                with act.Fori(0, pairs) as i:
                    for s in range(2):
                        n0 = at + s + 1
                        act.wait_ge(raw_ready[n0 % 2], 16 * i + 16 * (n0 // 2 + 1))
                        act.wait_ge(filled, 2 * CT * i + (f0 + CT * s))
                        nact.activation(w_hi[:, n0 % 2, :], raw[:, n0 % 2, :], ACT.Copy).then_inc(hi_ready, 1)
                        for j in range(CT):
                            f = f0 + CT * s + j
                            if s == 0:
                                act.wait_ge(filled, 2 * CT * i + (f + 1))
                                act.wait_ge(taken[f % 2], CT * i + f // 2)
                                nact.activation(two[:, j, :], bank[f % 2][:, :], ACT.Silu).then_inc(taken[f % 2], 1)
                            else:
                                act.wait_ge(taken[f % 2], CT * i + (f // 2 + 1))
                                nact.activation(a_hi[:, bass.ds(CT * i + j, 1), :], a32[:, j:j + 1, :], ACT.Copy)\
                                    .then_inc(S["a_hi_ready"], 1)
                for c in range(down_at[part], part_at[1] if part == 0 else NC):
                    if c + 1 < NC:
                        split(c + 1)

        @block.vector
        def _(dve):
            vec = nc.vector
            steps = [0]

            def link(ins):
                steps[0] += 1
                ins.then_inc(S["dve_step"], 1)
                dve.wait_ge(S["dve_step"], steps[0])

            def split(c):
                n = chunks[c][2] * chunks[c][3]
                dve.wait_ge(hi_ready, c + 1)
                vec.tensor_tensor(w_lo[:, c % 2, 0:n], raw[:, c % 2, 0:n], w_hi[:, c % 2, 0:n].bitcast(F32),
                                  ALU.subtract).then_inc(lo_ready, 1)

            def split_half(c, second):
                n = chunks[c][2] * chunks[c][3] // 2
                part = slice(n * second, n * (second + 1))
                dve.wait_ge(hi_ready, c + 1)
                ins = vec.tensor_tensor(w_lo[:, c % 2, part], raw[:, c % 2, part], w_hi[:, c % 2, part].bitcast(F32),
                                        ALU.subtract)
                ins.then_inc(lo_ready if second else S["dve_step"], 1)
                steps[0] += not second

            roots = [0]

            def inverse_root(at):
                roots[0] += 1
                dve.wait_ge(S["root_ready"], roots[0])
                a, v, r, w = newton[:, at], stat[:, at], rstd[:, at], root[:, at]
                link(vec.reciprocal(r, w))
                link(vec.tensor_tensor(a, r, r, ALU.mult))
                link(vec.tensor_tensor(a, a, v, ALU.mult))
                link(vec.tensor_scalar(a, a, -0.5, 1.5, ALU.mult, ALU.add))
                vec.tensor_tensor(r, r, a, ALU.mult).then_inc(S["rstd_ready"], 1)
                dve.wait_ge(S["rstd_ready"], roots[0])

            for t in (1, 3):
                dve.wait_ge(x_ready[t], 16)
                link(vec.tensor_tensor_reduce(out=dve_junk[:, t // 2, :], in0=x_sb[:, t, :], in1=x_sb[:, t, :], scale=1.0,
                                              scalar=0.0, op0=ALU.mult, op1=ALU.add, accum_out=stat[:, t:t + 1]))
            dve.wait_ge(S["squares_summed"], 2)
            vec.tensor_scalar(stat[:, 0:TT], stat[:, 0:TT], 1.0 / D, EPS, ALU.mult, ALU.add).then_inc(S["var_ready"], 1)
            inverse_root(slice(0, TT))
            for t in range(TT - 1):
                vec.tensor_scalar(x_sb[:, t, :], x_sb[:, t, :], rstd[:, t:t + 1], None, ALU.mult)\
                    .then_inc(S["h_scaled"], 1)
            split(0)
            for k in range(KT):
                dve.wait_ge(S["h_hi_ready"], k + 1)
                vec.scalar_tensor_tensor(out=h_lo[:, k, :], in0=bank[2 + k % 6][:, :],
                                         scalar=vcol[:, MIXN + k:MIXN + k + 1], in1=h_hi[:, k, :].bitcast(F32),
                                         op0=ALU.mult, op1=ALU.subtract).then_inc(S["h_lo_ready"], 1)

            def constants():
                dve.wait_ge(S["const_made"], 5)
                vec.tensor_copy(one_r[:, :], neg_one[:, :])
                vec.tensor_copy(tri_r[:, :], neg_tri[:, :]).then_inc(S["signs_ready"], 1)
                dve.wait_ge(S["corr_made"], 1)
                link(vec.reciprocal(ramp[:, :, :], ramp[:, :, :]))
                for i in range(MT):
                    link(vec.tensor_scalar(ramp[:, i, :], ramp[:, i, :], window[:, i:i + 1], None, ALU.mult))

            def stack_low(queries, src, heads, tiles, scale):
                for x in range(2):
                    own, other = slice(64 * x, 64 * x + 64), slice(64 - 64 * x, 128 - 64 * x)
                    if queries:
                        ins = vec.scalar_tensor_tensor(out=q_lo[own, tiles, :], in0=src[own], scalar=scale,
                                                       in1=q_stack[own, heads(x), :].bitcast(F32),
                                                       op0=ALU.mult, op1=ALU.subtract)
                    else:
                        ins = vec.tensor_tensor(k_stack[other, heads(x), :], src[own],
                                                k_stack[own, heads(x), :].bitcast(F32), ALU.subtract)
                return ins

            def indexer(b):
                w = P * (b + 1)
                acc = score[:, score_at[b]:score_at[b] + w]
                for h in range(IDX_HEADS):
                    n = IDX_HEADS * (b - 1) + h
                    dve.wait_ge(S["relu_ready"], n + 1)
                    if h > 0:
                        dve.wait_ge(S["relu_used"], n)
                    vec.scalar_tensor_tensor(out=acc, in0=relu[:, n % 4, 0:w], scalar=iw[:, b, h:h + 1],
                                             in1=causal[:, SEQ - w:SEQ] if h == 0 else acc,
                                             op0=ALU.mult, op1=ALU.add).then_inc(S["relu_used"], 1)
                dve.wait_ge(S["relu_used"], IDX_HEADS * b)

            def take_top(b, rounds, last=False):
                w = P * (b + 1)
                acc = score[:, score_at[b]:score_at[b] + w]
                for _ in range(rounds):
                    link(vec.max(best[:, :], acc))
                    link(vec.match_replace(acc, best[:, :], acc, TAKEN))
                if last:
                    vec.tensor_scalar(acc, acc, BETWEEN, MASKED, ALU.is_gt, ALU.mult).then_inc(S["bias_ready"], 1)

            def norm_qk():
                wait_chunk_taken(dve, 3)
                for which in range(2):
                    v = qk[:, which]
                    link(vec.tensor_tensor(sq_tmp[:, :, :], v, v, ALU.mult))
                    link(vec.tensor_reduce(stat[:, 16 * which:16 * which + 16],
                                           sq_tmp[:, :, :].rearrange("p t (h e) -> p (t h) e", h=HEADS), AX.X, ALU.add))
                vec.tensor_scalar(stat[:, :], stat[:, :], 1.0 / HEAD_DIM, EPS, ALU.mult, ALU.add)\
                    .then_inc(S["var_ready"], 1)
                inverse_root(slice(0, 32))
                link(vec.tensor_scalar(rstd[:, 0:16], rstd[:, 0:16], SCALE, None, ALU.mult))
                for which in range(2):
                    v = qk[:, which].rearrange("p t (h e) -> p (t h) e", h=HEADS)
                    r = rstd[:, 16 * which:16 * which + 16].unsqueeze(2).broadcast_to([P, 16, HEAD_DIM])
                    vec.tensor_tensor(v, v, r, ALU.mult).then_inc(S["qk_scaled"], 1)

            def norm_gv():
                wait_chunk_taken(dve, 5)
                for t in range(TT):
                    link(vec.bn_stats(bn[:, t, :], gv[:, t, :]))
                for t in range(TT):
                    link(vec.bn_aggr(mv[:, t, :], bn[:, t, :]))
                vec.tensor_scalar(stat[:, 0:TT], mv[:, :, 1], EPS, None, ALU.add).then_inc(S["var_ready"], 1)
                inverse_root(slice(0, TT))
                for t in range(TT):
                    vec.tensor_scalar(gv[:, t, :], gv[:, t, :], mv[:, t, 0:1], rstd[:, t:t + 1], ALU.subtract,
                                      ALU.mult).then_inc(S["v_normed"], 1)

            def gate_mixed():
                dve.wait_ge(S["mix_filled"], 1)
                dve.wait_ge(S["gb_in"], 64)
                wait_chunk_taken(dve, 6)
                for i in range(MT):
                    out3 = mixed[:, i, :].rearrange("p (n t) -> p n t", n=TT)
                    link(vec.scalar_tensor_tensor(out=out3, in0=bank[6 + i][:, :].rearrange("p (n t) -> p n t", n=TT),
                                                  scalar=vcol[:, GMN + i:GMN + i + 1],
                                                  in1=gb[:, i:i + 1, :].broadcast_to([P, TT, P]),
                                                  op0=ALU.mult, op1=ALU.add))
                vec.tensor_tensor(mixed[:, :, :], mixed[:, :, :], gu[:, :, :], ALU.mult).then_inc(S["mixed_ready"], 1)
                for i in range(MT):
                    dve.wait_ge(S["o_hi_ready"], i + 1)
                    vec.tensor_tensor(o_lo[:, O_SET[0], i, :], mixed[:, i, :], o_hi[:, O_SET[0], i, :].bitcast(F32),
                                      ALU.subtract).then_inc(S["o_lo_ready"], 1)

            def pool_means():
                dve.wait_ge(S["windows_summed"], 1)
                tiles = ((s2, 0, 0), (s4, 0, 1), (s8, 0, 0), (s16, 0, 1))
                for g, (s, i, up) in enumerate(tiles):
                    r = slice(64 * up, 64 * up + 64)
                    link(vec.tensor_tensor(s[r, i, PAD:2 * PAD], s[r, i, PAD:2 * PAD], ramp[r, g // 2, :], ALU.mult))
                for g, (s, i, up) in enumerate(tiles):
                    r = slice(64 * up, 64 * up + 64)
                    last = vec.scalar_tensor_tensor(out=s[r, i, PAD:PW], in0=s[r, i, PAD:PW],
                                                    scalar=inv_window[r, g // 2:g // 2 + 1], in1=pin[r, g // 2, PAD:PW],
                                                    op0=ALU.mult, op1=ALU.subtract)
                last.then_inc(S["pooled_ready"], 1)

            def out_parts(branch, b0, scale):
                for i in range(MT):
                    dve.wait_ge(S["o_hi_ready"], O_DONE[branch] - MT + i + 1)
                    hi = o_hi[:, O_SET[branch], i, :].bitcast(F32)
                    lo = o_lo[:, O_SET[branch], i, :]
                    if scale is None:
                        ins = vec.tensor_tensor(lo, bank[b0 + i][:, :], hi, ALU.subtract)
                    else:
                        ins = vec.scalar_tensor_tensor(out=lo, in0=bank[b0 + i][:, :],
                                                       scalar=vcol[:, scale + i:scale + i + 1], in1=hi,
                                                       op0=ALU.mult, op1=ALU.subtract)
                    ins.then_inc(S["o_lo_ready"], 1)

            def stick(h):
                dve.wait_ge(S["softplus_ready"], h + 1)
                for i, (a, z) in enumerate(((0, 512), (512, 1024), (1024, 1280))):
                    vec.scalar_tensor_tensor(out=stick_buf[:, a:z], in0=bank[2 + 3 * (h % 2) + i][:, 0:z - a],
                                             scalar=0.0, in1=stick_buf[:, a:z], op0=ALU.max, op1=ALU.add)\
                        .then_inc(S["stick_ready"], 1)

            def stick_low(h):
                for i, (a, z) in enumerate(((0, 512), (512, 1024), (1024, 1280))):
                    dve.wait_ge(S["stick_hi_ready"], 3 * h + i + 1)
                    vec.tensor_tensor(stick_lo[:, a:z], stick_buf[:, a:z], stick_hi[:, a:z].bitcast(F32), ALU.subtract)\
                        .then_inc(S["stick_lo_ready"], 1)

            def stick_out(h):
                dve.wait_ge(S["o_hi_ready"], O_DONE[1] + h + 1)
                r = slice(64 * (h % 2), 64 * (h % 2) + 64)
                vec.tensor_tensor(o_lo[r, O_SET[2], h // 2, :], bank[2 + 3 * (h % 2)][r, :],
                                  o_hi[r, O_SET[2], h // 2, :].bitcast(F32), ALU.subtract).then_inc(S["o_lo_ready"], 1)

            def biased(b):
                w = P * (b + 1)
                bias = causal[:, SEQ - P:SEQ] if b == 0 else score[:, score_at[b]:score_at[b] + w]
                if b >= 1:
                    dve.wait_ge(S["bias_ready"], b)
                    dve.wait_ge(S["prob_turned"], HEADS * b)
                else:
                    dve.wait_ge(S["sb_out"], HEADS)
                for h in range(HEADS):
                    dve.wait_ge(S["logits_filled"], HEADS * b + h + 1)
                    vec.tensor_tensor_reduce(out=prob[:, h, 0:w], in0=bank[2 + h][:, 0:w], in1=bias, scale=1.0,
                                             scalar=TAKEN, op0=ALU.add, op1=ALU.max,
                                             accum_out=top_logit[:, h:h + 1]).then_inc(S["biased_ready"], 1)

            def normalised(b):
                w = P * (b + 1)
                dve.wait_ge(S["prob_summed"], HEADS * (b + 1))
                link(vec.reciprocal(inv_total[:, :], total[:, :]))
                for h in range(HEADS):
                    vec.tensor_scalar(prob[:, h, 0:w], prob[:, h, 0:w], inv_total[:, h:h + 1], None, ALU.mult)\
                        .then_inc(S["prob_ready"], 1)


            rounds = {5: (1, 4), 6: (1, 6), 7: (1, 3), 8: (1, 3), 9: (2, 4), 10: (2, 3), 11: (2, 3), 12: (2, 3),
                      13: (2, 3), 16: (3, 4), 17: (3, 4), 18: (3, 4), 21: (3, 4)}
            assert all(sum(r for b, r in rounds.values() if b == i) * 8 == TOPK for i in (1, 2, 3))

            def slot(c):
                if c == 0:
                    constants()
                if IDX_SLOT <= c < IDX_SLOT + 3:
                    if c == IDX_SLOT:
                        dve.wait_ge(S["iw_ready"], 1)
                        dve.wait_ge(S["const_made"], 6)
                    indexer(c - IDX_SLOT + 1)
                    if c == 3:
                        norm_qk()
                if c == 5:
                    norm_gv()
                if c == 7:
                    gate_mixed()
                if c == 8:
                    pool_means()
                if c == 9:
                    out_parts(1, 6, PSC)
                if D_SLOT <= c < D_SLOT + HEADS + 2:
                    k = c - D_SLOT
                    if k >= 2:
                        stick_out(k - 2)
                    if k < HEADS:
                        stick(k)
                        stick_low(k)
                    if k == HEADS + 1:
                        dve.wait_ge(S["q_hi_ready"], MT + 1)
                        stack_low(True, qT, lambda x: slice(x, HEADS, 2), slice(0, MT), 1.0)
                        dve.wait_ge(S["k_hi_ready"], MT + 1)
                        stack_low(False, kT, lambda x: slice(x, HEADS, 2), None, 1.0).then_inc(S["stacks_ready"], 1)
                if c in rounds:
                    b, n = rounds[c]
                    take_top(b, n, last=all(rounds[d][0] > b for d in rounds if d > c))
                if A_SLOT <= c <= A_SLOT + 2 * TT:
                    b, odd = (c - A_SLOT) // 2, (c - A_SLOT) % 2
                    if not odd and b < TT:
                        biased(b)
                        normalised(b)
                    elif not odd:
                        out_parts(3, 6, None)

            for c in range(MIXER_CHUNKS):
                kind, _, _, _, what = chunks[c]
                if c + 1 < MIXER_CHUNKS and kind != "proj" and not split_early(c + 1):
                    split(c + 1)
                if what == "ik":
                    dve.wait_ge(S["ik_hi_ready"], 1)
                    vec.tensor_tensor(ik_stack[64:96, :], bank[0][0:32, :], ik_stack[0:32, :].bitcast(F32),
                                      ALU.subtract).then_inc(taken[0], 1)
                if what == "iq":
                    for j in range(MT):
                        dve.wait_ge(S["iq_hi_ready"], j + 1)
                        b = (fill_at[c] + j) % 2
                        vec.tensor_tensor(iq_lo[:, j, :], bank[b][:, :], iq_hi[:, j, :].bitcast(F32),
                                          ALU.subtract).then_inc(taken[b], 1)
                if what in ("sq", "sk"):
                    for j in range(MT):
                        dve.wait_ge(S["q_hi_ready" if what == "sq" else "k_hi_ready"], j + 1)
                        b = (fill_at[c] + j) % 2
                        stack_low(what == "sq", bank[b], lambda x: 2 * j + x, j, SCALE).then_inc(taken[b], 1)
                if split_early(c + 2):
                    split(c + 2)
                if kind == "proj":
                    for d in range(KT):
                        if d in (2, 5):
                            split_half(c + 1, d == 5)
                        f = fill_at[c] + d
                        dve.wait_ge(filled, f + 1)
                        if d == 0:
                            wait_chunk_taken(dve, c - 1)
                        y = (what - 1) * KT + d
                        if what > 0 and y >= 2:
                            dve.wait_ge(S["proj_added"], y - 1)
                        dst = merged[:, d, :] if what == 0 else two[:, y % 2, :]
                        vec.tensor_tensor(dst, bank[f % 2][:, :], gates[:, d, :], ALU.mult)\
                            .then_inc(taken[f % 2], 1)
                    if what == N_BRANCH - 1:
                        for d in range(KT):
                            dve.wait_ge(S["mg_hi_ready"], d + 1)
                            vec.tensor_tensor(h_lo[:, d, :], merged[:, d, :], h_hi[:, d, :].bitcast(F32), ALU.subtract)\
                                .then_inc(S["mg_lo_ready"], 1)
                if kind == "acc" and what[0] == 0 and what[3]:
                    for t in range(TT):
                        a = what[0] * TT + t
                        dve.wait_ge(S["acc_filled"], a + 1)
                        if a == 0:
                            dve.wait_ge(S["x_back"], 16)
                        v = x_sb[:, t, (what[0] % 2) * HALF:(what[0] % 2 + 1) * HALF]
                        vec.tensor_tensor(v, v, acc_bank(a)[:, :], ALU.add).then_inc(S["x1_taken"], 1)
                slot(c)

            def h2_low(t):
                for half in range(2):
                    dve.wait_ge(S["h2_hi_ready"], 2 * t + half + 1)
                    ks = slice(half * KT // 2, (half + 1) * KT // 2)
                    vec.tensor_tensor(h_lo[:, ks, t * P:(t + 1) * P],
                                      bank[4 + half][:, :].rearrange("p (k t) -> p k t", t=P),
                                      h_hi[:, ks, t * P:(t + 1) * P].bitcast(F32), ALU.subtract)\
                        .then_inc(S["h2_lo_ready"], 1)

            dve.wait_ge(S["squares_summed"], 2 + TT)
            link(vec.tensor_scalar(stat[:, 0:TT], sums[:, 0:TT], 1.0 / D, EPS, ALU.mult, ALU.add))
            dve.wait_ge(S["gain_in"], 16)
            for t in range(TT):
                a = TT + t
                dve.wait_ge(S["acc_filled"], a + 1)
                v = x_sb[:, t, HALF:D]
                vec.tensor_tensor(v, v, acc_bank(a)[:, :], ALU.add).then_inc(S["x1_taken"], 1)
                if t == 2:
                    split(MIXER_CHUNKS)
                dve.wait_ge(S["squares_summed"], 2 + a + 1)
                vec.tensor_scalar(stat[:, t:t + 1], sums[:, a:a + 1], 1.0 / D, stat[:, t:t + 1], ALU.mult, ALU.add)\
                    .then_inc(S["var_ready"], 1)
                inverse_root(slice(t, t + 1))
                vec.scalar_tensor_tensor(out=h2[:, t, :], in0=x_sb[:, t, :], scalar=rstd[:, t:t + 1], in1=ffn_gain[:, :],
                                         op0=ALU.mult, op1=ALU.mult).then_inc(S["h2_scaled"], 1)
                if t > 0:
                    h2_low(t - 1)
            h2_low(TT - 1)

            for part, pairs in enumerate(PAIRS):
                at, f0 = part_at[part], fill_at[part_at[part]]
                hid = CT * part * PAIRS[0]
                with dve.Fori(0, pairs) as i:
                    for s in range(2):
                        nslot = (at + s + 1) % 2
                        dve.wait_ge(hi_ready, 2 * i + (at + s + 2))
                        vec.tensor_tensor(w_lo[:, nslot, :], raw[:, nslot, :], w_hi[:, nslot, :].bitcast(F32),
                                          ALU.subtract).then_inc(lo_ready, 1)
                        if s == 0:
                            continue
                        for j in range(CT):
                            f = f0 + CT * s + j
                            dve.wait_ge(filled, 2 * CT * i + (f + 1))
                            dve.wait_ge(taken[f % 2], CT * i + f // 2)
                            vec.tensor_tensor(a32[:, j, :], bank[f % 2][:, :], two[:, j, :], ALU.mult)\
                                .then_inc(taken[f % 2], 1)
                        for j in range(CT):
                            dve.wait_ge(S["a_hi_ready"], CT * i + (hid + j + 1))
                            vec.tensor_tensor(a_lo[:, bass.ds(CT * i + j, 1), :], a32[:, j:j + 1, :],
                                              a_hi[:, bass.ds(CT * i + j, 1), :].bitcast(F32), ALU.subtract)\
                                .then_inc(S["a_lo_ready"], 1)
                for c in range(down_at[part], part_at[1] if part == 0 else NC):
                    if c + 1 < NC:
                        split(c + 1)
                    group, _, _, last = chunks[c][4]
                    if last:
                        for t in range(TT):
                            a = group * TT + t
                            dve.wait_ge(S["acc_filled"], a + 1)
                            dve.wait_ge(S["x1_taken"], a + 1 - TT)
                            v = x_sb[:, t, (group % 2) * HALF:(group % 2 + 1) * HALF]
                            vec.tensor_tensor(v, v, acc_bank(a)[:, :], ALU.add).then_inc(S["x1_taken"], 1)

        @block.tensor
        def _(pe):
            mm = nc.tensor.matmul

            def three(dst, l_hi, l_lo, r_hi, r_lo, start, stop):
                mm(dst, l_hi, r_hi, start=start, stop=False)
                mm(dst, l_hi, r_lo, start=False, stop=False)
                return mm(dst, l_lo, r_hi, start=False, stop=stop)

            def take_bank(f):
                if f >= 2:
                    pe.wait_ge(taken[f % 2], f // 2)
                return bank[f % 2]

            def rows_chunk(slot_, cols, f0, wait_bank):
                for j in range(cols // P):
                    wait_bank(j)
                    b = bank[(f0 + j) % 2]
                    for k in range(KT):
                        w = slice(k * cols + j * P, k * cols + (j + 1) * P)
                        last = three(b[:, :], w_hi[:, slot_, w], w_lo[:, slot_, w], h_hi[:, k, :], h_lo[:, k, :],
                                     k == 0, k == KT - 1)
                    last.then_inc(filled, 1)

            def toks_chunk(slot_, f0, wait_bank, between):
                for j in range(2):
                    wait_bank(j)
                    for t in range(2):
                        if j or t:
                            between(2 * j + t)
                        rows = slice((2 * j + t) * P, (2 * j + t + 1) * P)
                        for k in range(KT):
                            w = slice(k * CW, (k + 1) * CW)
                            last = three(bank[(f0 + j) % 2][:, t * CW:(t + 1) * CW], h_hi[:, k, rows], h_lo[:, k, rows],
                                         w_hi[:, slot_, w], w_lo[:, slot_, w], k == 0, k == KT - 1)
                    last.then_inc(filled, 1)

            def proj_chunk(slot_, c, m):
                pe.wait_ge(S["o_lo_ready"], O_DONE[m])
                for d in range(KT):
                    b = take_bank(fill_at[c] + d)
                    for k in range(MT):
                        w = slice(k * D + d * P, k * D + (d + 1) * P)
                        last = three(b[:, :], w_hi[:, slot_, w], w_lo[:, slot_, w], o_hi[:, O_SET[m], k, :],
                                     o_lo[:, O_SET[m], k, :], k == 0, k == MT - 1)
                    last.then_inc(filled, 1)

            def acc_chunk(c, l_hi, l_lo):
                _, _, nk, _, (group, k0, first, last_) = chunks[c]
                for k in range(nk):
                    if group < 2:
                        pe.wait_ge(S["mg_lo_ready"], k0 + k + 1)
                    else:
                        pe.wait_ge(S["a_lo_ready"], (group // 2 - 1) * FF_PART + k0 + k + 1)
                    for t in range(TT):
                        a = group * TT + t
                        if first and k == 0 and a >= 6:
                            pe.wait_ge(S["x1_taken"], a - 5)
                        rows, w = slice(t * P, (t + 1) * P), slice(k * HALF, (k + 1) * HALF)
                        end = last_ and k == nk - 1
                        ins = three(acc_bank(a)[:, :], l_hi[:, k0 + k, rows], l_lo[:, k0 + k, rows],
                                    w_hi[:, c % 2, w], w_lo[:, c % 2, w], first and k == 0, end)
                        if end:
                            ins.then_inc(S["acc_filled"], 1)
                if not last_:
                    ins.then_inc(S["acc_chunks"], 1)

            pe.wait_ge(S["const_made"], 1)
            pe.wait_ge(S["vec_in"], 16 * 8)
            n = 2 * KT + 6
            nc.tensor.transpose(bank[1][:, 0:n], vrow[:, :], ident[0:n, 0:n]).then_inc(S["vec_turned"], 1)

            def turn_h(k):
                if k >= 6:
                    pe.wait_ge(S["h_lo_ready"], k - 5)
                for t in range(TT):
                    if k == 0 and t < TT - 1:
                        pe.wait_ge(S["h_scaled"], t + 1)
                    elif k == 0:
                        pe.wait_ge(S["h_last_scaled"], 1)
                    last = nc.tensor.transpose(bank[2 + k % 6][:, t * P:(t + 1) * P], x_sb[:, t, k * P:(k + 1) * P],
                                               ident[:, :])
                last.then_inc(S["h_turned"], 1)

            for k in range(6):
                turn_h(k)
            pe.wait_ge(hi_ready, 1)
            pe.wait_ge(lo_ready, 1)
            for k in range(KT):
                if k + 6 < KT:
                    turn_h(k + 6)
                pe.wait_ge(S["h_lo_ready"], k + 1)
                w = slice(k * P, (k + 1) * P)
                last = three(bank[0][:, :], w_hi[:, 0, w], w_lo[:, 0, w], h_hi[:, k, :], h_lo[:, k, :], k == 0, k == KT - 1)
            last.then_inc(filled, 1)

            def indexer(b, heads):
                if b == 1 and heads[0] == 0:
                    pe.wait_ge(S["iq_stacked"], 16 * 12)
                w = P * (b + 1)
                for h in heads:
                    n = IDX_HEADS * (b - 1) + h
                    if n >= 4:
                        pe.wait_ge(S["relu_ready"], n - 3)
                    mm(bank[2 + n % 4][:, 0:w], iq_stack[0:96, h, b * P:(b + 1) * P], ik_stack[0:96, 0:w],
                       start=True, stop=True).then_inc(S["idx_filled"], 1)

            def turn_qk():
                for i in range(4):
                    which, pair = i // 2, i % 2
                    pe.wait_ge(S["qk_scaled"], which + 1)
                    if which:
                        pe.wait_ge(S["qk_evac"], pair + 1)
                    for t in range(TT):
                        last = nc.tensor.transpose(bank[6 + pair][:, t * P:(t + 1) * P],
                                                   qk[:, which, t, pair * P:(pair + 1) * P], ident[:, :])
                    last.then_inc(S["qk_turned"], 1)

            def mix_chunks():
                pe.wait_ge(S["v_normed"], TT)
                pe.wait_ge(S["qk_evac"], 4)
                for g in range(4):
                    for n in range(TT):
                        last = mm(bank[6 + g // 2][64 * (g % 2):64 * (g % 2) + 64, n * P:(n + 1) * P],
                                  gv[:, n, g * 64:(g + 1) * 64], wsT[:, g, :], start=True, stop=True)
                last.then_inc(S["mix_filled"], 1)

            def pool_map():
                pe.wait_ge(S["pooled_ready"], 1)
                pe.wait_ge(S["pw_in"], 64)
                pe.wait_ge(S["mixed_ready"], 1)
                for g, (s, i) in enumerate(((s2, 0), (s4, 0), (s8, 0), (s16, 0))):
                    r = slice(64 * (g % 2), 64 * (g % 2) + 64)
                    last = mm(bank[6 + g // 2][r, :], pw[r, g // 2, :], s[r, i, PAD:PW], start=True, stop=True)
                last.then_inc(S["pool_filled"], 1)

            SB_AT = ((0, 0), (1, 0), (2, 0), (1, 384))
            SB_COL = (0, 512, 1024, 896)

            def sb_logits(h):
                r = slice(64 * (h % 2), 64 * (h % 2) + 64)
                if h >= 2:
                    pe.wait_ge(S["o_lo_ready"], O_DONE[1] + h - 1)
                for j in (0, 1, 3, 2):
                    b, a = SB_AT[j]
                    w = SEQ - j * P
                    dst = bank[2 + 3 * (h % 2) + b]
                    mm(dst[:, a:a + w], k_stack[:, h, j * P:(j + 1) * P], q_stack[:, h, j * P:SEQ],
                       start=(j != 3), stop=False, skip_group_check=True)
                    mm(dst[:, a:a + w], k_stack[r, h, j * P:(j + 1) * P], q_lo[r, h // 2, j * P:SEQ],
                       start=False, stop=False, skip_group_check=True)
                    last = mm(dst[:, a:a + P], identb[:, :], later[:, :], start=False, stop=True, skip_group_check=True)
                last.then_inc(S["sb_filled"], 1)

            def sb_tails(h):
                pe.wait_ge(S["stick_lo_ready"], 3 * (h + 1))
                for i in (0, 1, 3, 2):
                    b, a = SB_AT[i]
                    for j in range(i, TT):
                        w = SEQ - j * P
                        o = a + (j - i) * P
                        for part in (stick_hi, stick_lo):
                            last = mm(bank[2 + 3 * (h % 2) + b][:, o:o + w], (tri_r if i == j else one_r)[:, :],
                                      part[:, SB_COL[j]:SB_COL[j] + w], start=False, stop=True, skip_group_check=True)
                last.then_inc(S["tail_filled"], 1)

            def sb_values(h):
                pe.wait_ge(S["beta_ready"], 3 * (h + 1))
                r = slice(64 * (h % 2), 64 * (h % 2) + 64)
                for j in range(TT):
                    w = SEQ - j * P
                    last = mm(bank[2 + 3 * (h % 2)][r, j * P:SEQ], sv[:, j, h * 64:(h + 1) * 64],
                              beta[:, SB_COL[j]:SB_COL[j] + w], start=(j == 0), stop=(j == TT - 1), skip_group_check=True)
                last.then_inc(S["sb_out"], 1)

            def attn_logits(b):
                if b == 0:
                    pe.wait_ge(S["o_lo_ready"], O_DONE[2])
                else:
                    pe.wait_ge(S["probT_ready"], HEADS * b)
                w = P * (b + 1)
                for h in range(HEADS):
                    r = slice(64 * (h % 2), 64 * (h % 2) + 64)
                    mm(bank[2 + h][:, 0:w], q_stack[:, h, b * P:(b + 1) * P], k_stack[:, h, 0:w], start=True, stop=False)
                    mm(bank[2 + h][:, 0:w], q_lo[r, h // 2, b * P:(b + 1) * P], k_stack[r, h, 0:w],
                       start=False, stop=True).then_inc(S["logits_filled"], 1)

            def attn_turn(b):
                for h in range(HEADS):
                    pe.wait_ge(S["prob_ready"], HEADS * b + h + 1)
                    for j in range(b + 1):
                        last = nc.tensor.transpose(bank[2 + h][:, j * P:(j + 1) * P], prob[:, h, j * P:(j + 1) * P],
                                                   ident[:, :])
                    last.then_inc(S["prob_turned"], 1)

            def attn_values(b):
                for h in range(HEADS):
                    pe.wait_ge(S["probT_ready"], HEADS * b + h + 1)
                    r = slice(64 * (h % 2), 64 * (h % 2) + 64)
                    for j in range(b + 1):
                        last = mm(bank[6 + h // 2][r, b * P:(b + 1) * P], av[:, j, h * 64:(h + 1) * 64],
                                  probT[:, h, j * P:(j + 1) * P], start=(j == 0), stop=(j == b))
                last.then_inc(S["attn_out"], 1)

            def slot(c):
                if c == 1:
                    pe.wait_ge(S["tril_made"], 1)
                    for g in range(4):
                        last = nc.tensor.transpose(bank[7][:, g * P:(g + 1) * P], ws[:, g, :], ident[:, :])
                    last.then_inc(S["ws_turned"], 1)
                    pe.wait_ge(S["h_lo_ready"], KT)
                    wait_chunk_taken(pe, 0)
                    for t in range(TT):
                        last = nc.tensor.transpose(bank[6][:, t * IDX_HEADS:(t + 1) * IDX_HEADS],
                                                   ikw[32:32 + IDX_HEADS, t * P:(t + 1) * P],
                                                   ident[32:32 + IDX_HEADS, 32:32 + IDX_HEADS])
                    last.then_inc(S["iw_turned"], 1)
                if IDX_SLOT <= c < IDX_SLOT + 3:
                    indexer(c - IDX_SLOT + 1, range(0, 4))
                if c == 5:
                    pe.wait_ge(S["iw_ready"], 1)
                    pe.wait_ge(S["ws_ready"], 1)
                    turn_qk()
                if c == 6:
                    mix_chunks()
                if c == 9:
                    pool_map()
                if D_SLOT <= c < D_SLOT + HEADS + 2:
                    k = c - D_SLOT
                    if k == 0:
                        for done in (8, 9, 10):
                            wait_chunk_taken(pe, done)
                        pe.wait_ge(S["o_lo_ready"], O_DONE[1])
                        pe.wait_ge(S["relu_ready"], 3 * IDX_HEADS)
                        pe.wait_ge(S["signs_ready"], 1)
                    if k >= 2:
                        sb_values(k - 2)
                    if 1 <= k <= HEADS:
                        sb_tails(k - 1)
                    if k < HEADS:
                        sb_logits(k)
                if A_SLOT <= c <= A_SLOT + 2 * TT:
                    b, odd = (c - A_SLOT) // 2, (c - A_SLOT) % 2
                    if c == A_SLOT:
                        wait_chunk_taken(pe, 4)
                        pe.wait_ge(S["stacks_ready"], 1)
                    if odd:
                        attn_turn(b)
                    else:
                        if b > 0:
                            attn_values(b - 1)
                        if b < TT:
                            attn_logits(b)

            def between(c, step):
                if IDX_SLOT <= c - 1 < IDX_SLOT + 3 and step <= 2:
                    indexer(c - IDX_SLOT, range(2 + 2 * step, 4 + 2 * step))

            for c in range(1, MIXER_CHUNKS - 2):
                kind, _, _, cols, what = chunks[c]
                pe.wait_ge(hi_ready, c + 1)
                pe.wait_ge(lo_ready, c + 1)
                if kind == "rows":
                    rows_chunk(c % 2, cols, fill_at[c], lambda j: take_bank(fill_at[c] + j))
                elif kind == "toks":
                    toks_chunk(c % 2, fill_at[c], lambda j: take_bank(fill_at[c] + j), lambda step: between(c, step))
                elif kind == "proj":
                    proj_chunk(c % 2, c, what)
                else:
                    acc_chunk(c, h_hi, h_lo)
                slot(c)

            def turn_h2(t):
                pe.wait_ge(S["h2_scaled"], t + 1)
                if t > 0:
                    pe.wait_ge(S["h2_lo_ready"], 2 * t)
                for half in range(2):
                    for k in range(KT // 2):
                        d = (half * KT // 2 + k) * P
                        last = nc.tensor.transpose(bank[4 + half][:, k * P:(k + 1) * P], h2[:, t, d:d + P], ident[:, :])
                    last.then_inc(S["h2_turned"], 1)

            for pair in range(0, TT, 2):
                for c in range(MIXER_CHUNKS - 2, MIXER_CHUNKS):
                    k0 = chunks[c][4][1]
                    pe.wait_ge(hi_ready, c + 1)
                    pe.wait_ge(lo_ready, c + 1)
                    for t in (pair, pair + 1):
                        rows = slice(t * P, (t + 1) * P)
                        if k0 == 0 and pair:
                            pe.wait_ge(S["x1_taken"], TT + t - 5)
                        for k in range(KC):
                            w = slice(k * HALF, (k + 1) * HALF)
                            last = three(acc_bank(TT + t)[:, :], h_hi[:, k0 + k, rows], h_lo[:, k0 + k, rows],
                                         w_hi[:, c % 2, w], w_lo[:, c % 2, w], k0 + k == 0, k0 + k == KT - 1)
                        if k0 > 0:
                            last.then_inc(S["acc_filled"], 1)
                        elif t == TT - 1:
                            last.then_inc(S["acc_chunks"], 1)
                    if pair:
                        if k0 == 0:
                            pe.wait_ge(S["x1_taken"], TT)
                        turn_h2(k0 // KC)

            first, f0 = MIXER_CHUNKS, fill_at[MIXER_CHUNKS]
            pe.wait_ge(hi_ready, first + 1)
            pe.wait_ge(lo_ready, first + 1)
            for half in range(2):
                cols = slice(half * SEQ // 2, (half + 1) * SEQ // 2)
                pe.wait_ge(S["h2_lo_ready"], TT * (half + 1))
                for j in range(CT):
                    b = take_bank(f0 + j)
                    for k in range(KT):
                        w = slice(k * CW + j * P, k * CW + (j + 1) * P)
                        last = three(b[:, cols], w_hi[:, first % 2, w], w_lo[:, first % 2, w], h_hi[:, k, cols],
                                     h_lo[:, k, cols], k == 0, k == KT - 1)
                    if half == 0:
                        turn_h2(2 + j)
                    else:
                        last.then_inc(filled, 1)
            pe.wait_ge(hi_ready, first + 2)
            pe.wait_ge(lo_ready, first + 2)
            rows_chunk((first + 1) % 2, CW, f0 + CT, lambda j: take_bank(f0 + CT + j))

            for part, pairs in enumerate(PAIRS):
                at, f0 = part_at[part], fill_at[part_at[part]]
                with pe.Fori(1 - part, pairs) as i:
                    for s in range(2):
                        pe.wait_ge(hi_ready, 2 * i + (at + s + 1))
                        pe.wait_ge(lo_ready, 2 * i + (at + s + 1))
                        f = f0 + CT * s
                        rows_chunk((at + s) % 2, CW, f,
                                   lambda j: pe.wait_ge(taken[(f + j) % 2], CT * i + (f + j) // 2))
                for c in range(down_at[part], part_at[1] if part == 0 else NC):
                    pe.wait_ge(hi_ready, c + 1)
                    pe.wait_ge(lo_ready, c + 1)
                    acc_chunk(c, a_hi, a_lo)


_INS = ["x", "mix_norm", "w_in", "attn_q_norm", "attn_k_norm", "pool_w", "pool_scale", "gmlp_norm", "gmlp_w_s",
        "gmlp_b", "w_branch", "w_out", "ffn_norm", "w_ffn_gate", "w_ffn_up", "w_ffn_down"]


def kernel(**inputs):
    import numpy as _np
    import concourse.bacc as _bacc
    from concourse import mybir as _mybir
    from concourse.bass_utils import run_bass_kernel_spmd as _run

    nc = _bacc.Bacc("TRN2", target_bir_lowering=False, num_devices=1)
    arrays, args = {}, []
    for name in _INS:
        a = _np.ascontiguousarray(inputs[name])
        arrays[f"in_{name}_dram"] = a
        args.append(nc.dram_tensor(f"in_{name}_dram", a.shape, _mybir.dt.from_np(a.dtype), kind="ExternalInput").ap())
    shape = inputs["x"].shape
    args.append(nc.dram_tensor("out_0_dram", shape, _mybir.dt.float32, kind="ExternalOutput").ap())
    hybrid_layer(nc, *args)
    r = _run(nc, [arrays], core_ids=[0])
    return r.results[0]["out_0_dram"]
```
